# Optimizing a Trainium2 kernel written in Bass

```python
import jax, jax.numpy as jnp
from jax import lax
import numpy as np

D_MODEL = 2048
BATCH = 1
SEQ = 256
DEPTH = 2

HEAD_DIM = 64
ATTN_WIDTH = D_MODEL // 2
N_Q_HEADS = ATTN_WIDTH // HEAD_DIM
N_KV_HEADS = N_Q_HEADS // 4
Q_PER_KV = N_Q_HEADS // N_KV_HEADS
KV_WIDTH = N_KV_HEADS * HEAD_DIM
WINDOW = 128
ATTN_BLOCK = 128

SSM_WIDTH = D_MODEL - ATTN_WIDTH
SSM_HEAD_DIM = 64
SSM_HEADS = SSM_WIDTH // SSM_HEAD_DIM
SSM_GROUPS = 4
HEADS_PER_GROUP = SSM_HEADS // SSM_GROUPS
D_STATE = 128
CONV_WIDTH = 4
CHUNK = 128
CONV_CH = SSM_WIDTH + 2 * SSM_GROUPS * D_STATE

MIX_WIDTH = ATTN_WIDTH + SSM_WIDTH
SPLIT_SIZES = (ATTN_WIDTH, KV_WIDTH, KV_WIDTH, SSM_WIDTH, CONV_CH, SSM_HEADS)
IN_PROJ_WIDTH = sum(SPLIT_SIZES)
SPLIT_POINTS = tuple(int(s) for s in np.cumsum(SPLIT_SIZES)[:-1])

D_FF = ((8 * D_MODEL // 3 + 255) // 256) * 256
EPS = 1e-6
DT_MIN = 0.001
DT_MAX = 0.1

kernel_name = 'hybrid_swa_sink_mamba2_parallel_heads'

def rms_norm(x, w):
    xf = x.astype(jnp.float32)
    y = xf * lax.rsqrt(jnp.mean(xf * xf, axis=-1, keepdims=True) + EPS)
    return (y * w.astype(jnp.float32)).astype(x.dtype)

def alibi_slopes():
    h = np.arange(1, N_Q_HEADS + 1, dtype=np.float32)
    return jnp.asarray(np.power(np.float32(2.0), -8.0 * h / N_Q_HEADS), jnp.float32)

def sliding_window_attention(q, k, v, q_norm_w, k_norm_w, sinks):
    b, L = q.shape[0], q.shape[1]
    nb = L // ATTN_BLOCK
    q = rms_norm(q, q_norm_w)
    k = rms_norm(k, k_norm_w)
    qb = q.reshape(b, nb, ATTN_BLOCK, N_KV_HEADS, Q_PER_KV, HEAD_DIM)

    def band(t):
        tb = t.reshape(b, nb, ATTN_BLOCK, N_KV_HEADS, HEAD_DIM)
        prev = jnp.pad(tb, ((0, 0), (1, 0), (0, 0), (0, 0), (0, 0)))[:, :-1]
        return jnp.concatenate([prev, tb], axis=2)

    kb, vb = band(k), band(v)
    scores = jnp.einsum('bnqhgd,bnkhd->bnhgqk', qb, kb,
                        preferred_element_type=jnp.float32) * (HEAD_DIM ** -0.5)

    r = jnp.arange(ATTN_BLOCK)[:, None]
    j = jnp.arange(2 * ATTN_BLOCK)[None, :]
    dist = ATTN_BLOCK + r - j
    key_pos = (jnp.arange(nb)[:, None, None] - 1) * ATTN_BLOCK + j[None]
    valid = (dist >= 0)[None] & (dist < WINDOW)[None] & (key_pos >= 0)
    slopes = alibi_slopes().reshape(N_KV_HEADS, Q_PER_KV)
    bias = -slopes[:, :, None, None] * dist.astype(jnp.float32)
    scores = jnp.where(valid[None, :, None, None], scores + bias, -jnp.inf)

    sink = sinks.astype(jnp.float32).reshape(N_KV_HEADS, Q_PER_KV)[None, None, :, :, None, None]
    m = jnp.maximum(jnp.max(scores, axis=-1, keepdims=True), sink)
    p = jnp.exp(scores - m)
    probs = p / (jnp.sum(p, axis=-1, keepdims=True) + jnp.exp(sink - m))
    out = jnp.einsum('bnhgqk,bnkhd->bnqhgd', probs.astype(vb.dtype), vb)
    return out.reshape(b, L, ATTN_WIDTH)

def causal_depthwise_conv(u, w, bias):
    out = lax.conv_general_dilated(u, w[:, None, :], window_strides=(1,),
                                   padding=[(CONV_WIDTH - 1, 0)],
                                   dimension_numbers=('NWC', 'WIO', 'NWC'),
                                   feature_group_count=u.shape[-1])
    return out + bias

def ssd_chunked(xs, dt, a, bm, cm):
    b, L = xs.shape[0], xs.shape[1]
    nc = L // CHUNK
    x = xs.reshape(b, nc, CHUNK, SSM_GROUPS, HEADS_PER_GROUP, SSM_HEAD_DIM)
    dtc = dt.reshape(b, nc, CHUNK, SSM_GROUPS, HEADS_PER_GROUP)
    bc = bm.reshape(b, nc, CHUNK, SSM_GROUPS, D_STATE)
    cc = cm.reshape(b, nc, CHUNK, SSM_GROUPS, D_STATE)
    cum = jnp.cumsum(dtc * a.reshape(SSM_GROUPS, HEADS_PER_GROUP), axis=2)
    xdt = x * dtc[..., None]

    cum_t = jnp.moveaxis(cum, 2, -1)
    seg = cum_t[..., :, None] - cum_t[..., None, :]
    causal = jnp.tril(jnp.ones((CHUNK, CHUNK), dtype=bool))
    decay = jnp.exp(jnp.where(causal, seg, -jnp.inf))
    cb = jnp.einsum('bclgn,bcsgn->bcgls', cc, bc)
    y_diag = jnp.einsum('bcgkls,bcsgkp->bclgkp', cb[:, :, :, None] * decay, xdt)

    decay_to_end = jnp.exp(cum[:, :, -1:] - cum)
    states = jnp.einsum('bclgn,bclgk,bclgkp->bcgkpn', bc, decay_to_end, xdt)
    chunk_decay = jnp.exp(cum[:, :, -1])

    def step(h, inp):
        s_c, d_c = inp
        return h * d_c[..., None, None] + s_c, h

    init = jnp.zeros((b, SSM_GROUPS, HEADS_PER_GROUP, SSM_HEAD_DIM, D_STATE), states.dtype)
    _, prev = lax.scan(step, init, (jnp.moveaxis(states, 1, 0), jnp.moveaxis(chunk_decay, 1, 0)))
    prev = jnp.moveaxis(prev, 0, 1)

    y_off = jnp.einsum('bclgn,bcgkpn,bclgk->bclgkp', cc, prev, jnp.exp(cum))
    return (y_diag + y_off).reshape(b, L, SSM_HEADS, SSM_HEAD_DIM)

def mamba2_mixer(z, xbc, dt_raw, conv_w, conv_b, dt_bias, a_log, d_skip, norm_w):
    b, L = z.shape[0], z.shape[1]
    xbc = jax.nn.silu(causal_depthwise_conv(xbc, conv_w, conv_b)).astype(jnp.float32)
    xs = xbc[..., :SSM_WIDTH].reshape(b, L, SSM_HEADS, SSM_HEAD_DIM)
    bm = xbc[..., SSM_WIDTH:SSM_WIDTH + SSM_GROUPS * D_STATE].reshape(b, L, SSM_GROUPS, D_STATE)
    cm = xbc[..., SSM_WIDTH + SSM_GROUPS * D_STATE:].reshape(b, L, SSM_GROUPS, D_STATE)
    dt = jax.nn.softplus(dt_raw.astype(jnp.float32) + dt_bias.astype(jnp.float32))
    a = -jnp.exp(a_log.astype(jnp.float32))
    y = ssd_chunked(xs, dt, a, bm, cm) + d_skip.astype(jnp.float32)[:, None] * xs
    g = (y.reshape(b, L, SSM_WIDTH) * jax.nn.silu(z.astype(jnp.float32)))
    g = g.reshape(b, L, SSM_GROUPS, SSM_WIDTH // SSM_GROUPS)
    g = g * lax.rsqrt(jnp.mean(g * g, axis=-1, keepdims=True) + EPS)
    g = g.reshape(b, L, SSM_WIDTH) * norm_w.astype(jnp.float32)
    return g.astype(z.dtype)

def setup_inputs(seed: int = 0) -> dict:
    key = jax.random.key(seed)
    ks = jax.random.split(key, 20)
    f32 = jnp.float32

    def nrm(k, shape, scale):
        return jax.random.normal(k, shape, f32) * scale

    log_dt = jax.random.uniform(ks[9], (DEPTH, SSM_HEADS), f32,
                                float(np.log(DT_MIN)), float(np.log(DT_MAX)))
    dt0 = jnp.exp(log_dt)
    dt_bias = dt0 + jnp.log(-jnp.expm1(-dt0))
    return {
        'x': nrm(ks[0], (BATCH, SEQ, D_MODEL), 1.0),
        'attn_norm_w': 1.0 + nrm(ks[1], (DEPTH, D_MODEL), 0.02),
        'w_in': nrm(ks[2], (DEPTH, D_MODEL, IN_PROJ_WIDTH), D_MODEL ** -0.5),
        'q_norm_w': 1.0 + nrm(ks[3], (DEPTH, HEAD_DIM), 0.02),
        'k_norm_w': 1.0 + nrm(ks[4], (DEPTH, HEAD_DIM), 0.02),
        'sinks': nrm(ks[5], (DEPTH, N_Q_HEADS), 0.5),
        'conv_w': nrm(ks[6], (DEPTH, CONV_WIDTH, CONV_CH), CONV_WIDTH ** -0.5),
        'conv_b': nrm(ks[7], (DEPTH, CONV_CH), 0.02),
        'dt_bias': dt_bias,
        'a_log': jnp.log(jax.random.uniform(ks[8], (DEPTH, SSM_HEADS), f32, 1.0, 16.0)),
        'd_skip': 1.0 + nrm(ks[10], (DEPTH, SSM_HEADS), 0.1),
        'ssm_norm_w': 1.0 + nrm(ks[11], (DEPTH, SSM_WIDTH), 0.02),
        'w_out': nrm(ks[12], (DEPTH, MIX_WIDTH, D_MODEL), MIX_WIDTH ** -0.5),
        'ffn_norm_w': 1.0 + nrm(ks[13], (DEPTH, D_MODEL), 0.02),
        'w_gate': nrm(ks[14], (DEPTH, D_MODEL, D_FF), D_MODEL ** -0.5),
        'w_up': nrm(ks[15], (DEPTH, D_MODEL, D_FF), D_MODEL ** -0.5),
        'w_down': nrm(ks[16], (DEPTH, D_FF, D_MODEL), D_FF ** -0.5),
    }

def reference(x, attn_norm_w, w_in, q_norm_w, k_norm_w, sinks, conv_w, conv_b, dt_bias,
              a_log, d_skip, ssm_norm_w, w_out, ffn_norm_w, w_gate, w_up, w_down):
    b, L = x.shape[0], x.shape[1]
    for l in range(DEPTH):
        h = rms_norm(x, attn_norm_w[l])
        proj = h @ w_in[l]
        q, k, v, z, xbc, dt_raw = jnp.split(proj, SPLIT_POINTS, axis=-1)
        attn = sliding_window_attention(
            q.reshape(b, L, N_Q_HEADS, HEAD_DIM),
            k.reshape(b, L, N_KV_HEADS, HEAD_DIM),
            v.reshape(b, L, N_KV_HEADS, HEAD_DIM),
            q_norm_w[l], k_norm_w[l], sinks[l])
        ssm = mamba2_mixer(z, xbc, dt_raw, conv_w[l], conv_b[l], dt_bias[l], a_log[l],
                           d_skip[l], ssm_norm_w[l])
        mixed = jnp.concatenate([attn.astype(x.dtype), ssm.astype(x.dtype)], axis=-1) @ w_out[l]
        x = (x + mixed).astype(x.dtype)
        h = rms_norm(x, ffn_norm_w[l])
        ff = (jax.nn.silu(h @ w_gate[l]) * (h @ w_up[l])) @ w_down[l]
        x = (x + ff).astype(x.dtype)
    return x


_drawn_inputs = setup_inputs


def setup_inputs(seed=0):
    import zlib

    import numpy as np

    out = dict(_drawn_inputs(seed))
    spreads = {}
    factors = {'q_norm_w': 8.0,
     'k_norm_w': 8.0,
     'sinks': 87.978,
     'ssm_norm_w': 3.326,
     'ffn_norm_w': 3.181}
    for name, (base, spread) in spreads.items():
        noise = np.random.default_rng([zlib.crc32(name.encode()), seed]).standard_normal(out[name].shape)
        drawn = base * np.exp(spread * noise) if base else spread * noise
        out[name] = __import__('jax').numpy.asarray(drawn.astype(out[name].dtype))
    for name, factor in factors.items():
        out[name] = (out[name] * factor).astype(out[name].dtype)
    return out
```

```python
from contextlib import ExitStack

import concourse.bass as bass
from concourse import mybir

ALU = mybir.AluOpType
ACT = mybir.ActivationFunctionType
F32 = mybir.dt.float32
F32R = mybir.dt.float32r
BF16 = mybir.dt.bfloat16
AX_X = mybir.AxisListType.X

P = 128
N = 512
HEAD = 64
Q_PER_KV = 4
CONV_W = 4
EPS = 1e-6
NEG = -1.0e30
RING = 4
WARM = 12
LEAD = 3
B_, C_ = 2, 3
DVE_STEPS, POOL_STEPS, ACT_STEPS = 129, 20, 11


def hybrid_decoder(nc, x, attn_norm_w, w_in, q_norm_w, k_norm_w, sinks, conv_w, conv_b, dt_bias, a_log,
                   d_skip, ssm_norm_w, w_out, ffn_norm_w, w_gate, w_up, w_down, out):
    DEPTH, D, _ = w_in.shape
    T = x.shape[1] // P
    TOK = T * P
    KT = D // P
    HQ = sinks.shape[1]
    HKV = HQ // Q_PER_KV
    HS = dt_bias.shape[1]
    GROUPS = 4
    HPG = HS // GROUPS
    GW = HPG * HEAD
    FF = w_gate.shape[2]
    FCH = FF // N
    DCH = D // N
    CT = N // P
    PPG = KT // 2
    assert T == 2 and KT == 16 and HQ == 16 and HS == 16 and FF == FCH * N and PPG % RING == 0

    KV_COL = HQ * HEAD
    Z_COL = KV_COL + 2 * HKV * HEAD
    XBC_COL = Z_COL + HS * HEAD
    DT_COL = XBC_COL + conv_b.shape[1]
    IN_COLS = [XBC_COL + N * j for j in range(4)] + [KV_COL, 0, N, Z_COL, Z_COL + N]
    G_IN = len(IN_COLS)
    OUT_ROWS = [0, 2, 4, 8, 10, 6, 12, 14]

    P_OUT = G_IN * PPG
    P_FF = P_OUT + DCH * PPG
    P_LOOP = P_FF + 2 * PPG
    DOWN = DCH * CT // 2
    PER_FF = 2 * PPG + DOWN
    P_LAST = P_LOOP + (FCH - 1) * PER_FF
    PAIRS = P_LAST + DOWN

    EV_ACT = G_IN + FCH
    EV_DVE = DCH + FCH * DCH

    V_ATTN, V_FFN, V_SSM, V_CB, V_CW = 0, KT, 2 * KT, 2 * KT + 8, 2 * KT + 8 + 16
    V_Q = V_CW + CONV_W * 16
    V_K = V_Q + 1
    VROWS = V_K + 1
    SLOPES = [float(2.0 ** (-8.0 * (h + 1) / HQ)) for h in range(HQ)]

    ctx = ExitStack()
    with ctx:
        def sb(name, shape, dt=F32):
            return ctx.enter_context(nc.sbuf_tensor(name, shape, dt))

        def sem(name):
            return ctx.enter_context(nc.semaphore(name))

        ps = ctx.enter_context(nc.psum_tensor("ps", [P, 8, N], F32))

        raw = sb("raw", [P, RING, 2, N])
        w_hi = sb("w_hi", [P, RING, 2, N], F32R)
        w_lo = sb("w_lo", [P, RING, 2, N], F32R)
        xr = sb("xr", [P, T, D])
        h_hi = sb("h_hi", [P, KT, TOK], F32R)
        h_lo = sb("h_lo", [P, KT, TOK], F32R)
        m_hi = sb("m_hi", [P, KT, TOK], F32R)
        m_lo = sb("m_lo", [P, KT, TOK], F32R)
        stage = sb("stage", [P, 2, T, N])
        ident = sb("ident", [P, P])
        identb = sb("identb", [P, P], BF16)
        tri = sb("tri", [P, P])
        ones = sb("ones", [P, P])
        maskb = sb("maskb", [P, HPG, P], BF16)
        dist = sb("dist", [P, 3 * P])
        MEANS = [D, HEAD, GW]
        numbers = sb("numbers", [P, 8])
        vrows = sb("vrows", [VROWS, P])
        vecs = sb("vecs", [P, VROWS])
        qw = sb("qw", [P, 1])
        dtb = sb("dtb", [P, HS])
        alog = sb("alog", [P, HS])
        dskip = sb("dskip", [P, HS])
        sink = sb("sink", [P, HQ])
        wdt = sb("wdt", [P, KT, HS])
        wdt_s = sb("wdt_s", [P, KT * 2 * HS + P - 2 * HS], F32R)
        wdt_parts = wdt_s[:, 0:KT * 2 * HS].rearrange("p (k a h) -> p k a h", a=2, h=HS)
        dtT = sb("dtT", [P, TOK])
        ssx = sb("ssx", [P, T, DCH])
        xsum = sb("xsum", [P, T])
        rsv = sb("rsv", [P, T])
        rs = sb("rs", [P, T])
        ssq = sb("ssq", [P, T, 8])
        rqv = sb("rqv", [P, T, 8])
        rq = sb("rq", [P, T, 8])
        ssg = sb("ssg", [P, 2, T, 2])
        rgv = sb("rgv", [P, T, 2])
        rg = sb("rg", [P, T, 2])
        acc = sb("acc", [P, CT, TOK])
        bt = sb("bt", [P, GROUPS, TOK])
        ctm = sb("ctm", [P, GROUPS, TOK])
        ys = sb("ys", [P, T, HS * HEAD])
        btok = sb("btok", [P, GROUPS, P])
        xdt = sb("xdt", [P, 2, GW])
        xde = sb("xde", [P, GW])
        dx = sb("dx", [P, 2, GW])
        state = sb("state", [P, GW])
        decay = sb("decay", [P, 2, HPG, P])
        dtx = sb("dtx", [P, T, HS])
        dta_ = sb("dta", [P, T, HS])
        dt = sb("dt", [P, T, HS])
        ea = sb("ea", [P, HS])
        sp = sb("sp", [P, 6, T, HS])
        cums = sb("cums", [P, 3, HS])
        ncum = sb("ncum", [P, T, HS])
        crest = sb("crest", [P, T, HS])
        PIECE = 32
        cpart = sb("cpart", [P, T, 4, PIECE], BF16)
        cumT = sb("cumT", [P, TOK], BF16)
        pick = sb("pick", [P, HS], BF16)
        togo = sb("togo", [P, HS])
        ecum = sb("ecum", [P, HS])
        dte = sb("dte", [P, HS])
        vaug = sb("vaug", [P, T, HKV, HEAD + 1])
        kT = sb("kT", [P, HKV, TOK])
        qT = sb("qT", [P, HQ // 2, TOK])
        sc = sb("sc", [P, 2, 2, 3 * P])
        pT = sb("pT", [P, 2, 3 * P])
        ao = sb("ao", [P, 2, T, P])
        mx = sb("mx", [P, 4, 2, T])
        es = sb("es", [P, 2, 2, T])
        den = sb("den", [P, 2, 2, T])

        raw_landed = [sem(f"raw_landed{i}") for i in range(RING)]
        hi_split = sem("hi_split")
        lo_split = sem("lo_split")
        pair_used = sem("pair_used")
        act_evac = sem("act_evac")
        dve_evac = sem("dve_evac")
        x_landed = [sem(f"x_landed{n}") for n in range(4)]
        rows_landed = sem("rows_landed")
        params_landed = sem("params_landed")
        set_up, ident_ready, const_ready = sem("set_up"), sem("ident_ready"), sem("const_ready")
        vec_psum, vec_ready = sem("vec_psum"), sem("vec_ready")
        xT_psum, h_hi_ready, h_lo_ready = sem("xT_psum"), sem("h_hi_ready"), sem("h_lo_ready")
        x_squares, x_sums, rs_ready = sem("x_squares"), sem("x_sums"), sem("rs_ready")
        wdt_hi_ready, wdt_lo_ready, dt_psum = sem("wdt_hi_ready"), sem("wdt_lo_ready"), sem("dt_psum")
        dtT_ready, dt_turned = sem("dtT_ready"), sem("dt_turned")
        cpart_ready, cumT_psum, cumT_ready = sem("cpart_ready"), sem("cumT_psum"), sem("cumT_ready")
        dt_abs, dt_exp, dta_ready = sem("dt_abs"), sem("dt_exp"), sem("dta_ready")
        cum_psum, cum_ready, ecum_ready = sem("cum_psum"), sem("cum_ready"), sem("ecum_ready")
        ch_psum, conv_ready, silu_ready = sem("ch_psum"), sem("conv_ready"), sem("silu_ready")
        tok_psum, tok_ready = sem("tok_psum"), sem("tok_ready")
        seg_psum, decay_ready, mt_ready = sem("seg_psum"), sem("decay_ready"), sem("mt_ready")
        xdt_ready, y_psum, state_ready, y_ready = sem("xdt_ready"), sem("y_psum"), sem("state_ready"), sem("y_ready")
        qk_squares, qk_sums, qk_scaled = sem("qk_squares"), sem("qk_sums"), sem("qk_scaled")
        qkT_psum, qkT_ready = sem("qkT_psum"), sem("qkT_ready")
        sc_psum, sc_ready, p_ready, pT_psum = sem("sc_psum"), sem("sc_ready"), sem("p_ready"), sem("pT_psum")
        pT_act, pT_dve, pv_psum, ao_ready = sem("pT_act"), sem("pT_dve"), sem("pv_psum"), sem("ao_ready")
        aoT_psum, ma_hi, ma_lo = sem("aoT_psum"), sem("ma_hi"), sem("ma_lo")
        gated, g_squares, g_normed = sem("gated"), sem("g_squares"), sem("g_normed")
        gT_psum, mg_hi, mg_lo = sem("gT_psum"), sem("mg_hi"), sem("mg_lo")
        ff_ready, ffT_psum, ff_hi, ff_lo = sem("ff_ready"), sem("ffT_psum"), sem("ff_hi"), sem("ff_lo")
        stored = sem("stored")
        dve_step, pool_step, act_step = sem("dve_step"), sem("pool_step"), sem("act_step")

        class Steps:
            def __init__(self, eng, s, per_layer):
                self.eng, self.s, self.per, self.n = eng, s, per_layer, 0

            def done(self, layer, ins):
                self.n += 1
                ins.then_inc(self.s, 1)
                self.eng.wait_ge(self.s, layer * self.per + self.n)

            def check(self):
                assert self.n == self.per, (self.s, self.n)

        def load_x(eng, n):
            cols = slice(n * N, (n + 1) * N)
            eng.dma_start(xr[:, :, cols], x[0, :, cols].rearrange("(t p) d -> p t d", p=P)).then_inc(x_landed[n], 16)

        block = ctx.enter_context(nc.Block())

        @block.sync
        def _(sp):
            load_x(sp, 0)

            def load_pair(slot, pair, source):
                sp.wait_ge(lo_split, pair + 1)
                sp.dma_start(raw[:, slot, :, :], source.rearrange("o (k p) n -> p (o k) n", p=P)) \
                    .then_inc(raw_landed[slot], 16)

            with sp.Fori(0, DEPTH) as layer:
                one = bass.ds(layer, 1)
                base = layer * PAIRS
                for q in range(PPG):
                    load_pair(q % RING, base + q, w_in[one, 2 * q * P:2 * (q + 1) * P, XBC_COL:XBC_COL + N])
                    if q == 1:
                        rows = [(V_ATTN, attn_norm_w, KT), (V_FFN, ffn_norm_w, KT), (V_SSM, ssm_norm_w, 8),
                                (V_CB, conv_b, 16)]
                        for at, src, n in rows:
                            sp.dma_start(vrows[at:at + n, :], src[one, :].rearrange("o (r p) -> (o r) p", p=P)) \
                                .then_inc(rows_landed, 16)
                        sp.dma_start(vrows[V_CW:V_CW + CONV_W * 16, :],
                                     conv_w[one, :, :].rearrange("o w (r p) -> (o w r) p", p=P)).then_inc(rows_landed, 16)
                        for at, src in ((V_Q, q_norm_w), (V_K, k_norm_w)):
                            sp.dma_start(vrows[at:at + 1, :].rearrange("o (w d) -> o w d", w=2),
                                         src[one, :].unsqueeze(1).broadcast_to([1, 2, HEAD])).then_inc(rows_landed, 16)
                for g, start, steps in ((0, 1, 4), (4, 0, 1), (5, 0, 2), (7, 0, 2)):
                    with sp.Fori(start, steps) as i:
                        for q in range(PPG):
                            load_pair(q % RING, base + i * PPG + (g * PPG + q),
                                      w_in[one, 2 * q * P:2 * (q + 1) * P, bass.ds(i * N + IN_COLS[g], N)])
                with sp.Fori(0, DCH) as n:
                    for q, r in enumerate(OUT_ROWS):
                        load_pair(q % RING, base + n * PPG + (P_OUT + q),
                                  w_out[one, r * P:(r + 2) * P, bass.ds(n * N, N)])
                for w, first in ((w_gate, P_FF), (w_up, P_FF + PPG)):
                    for q in range(PPG):
                        load_pair(q % RING, base + (first + q), w[one, 2 * q * P:2 * (q + 1) * P, 0:N])
                with sp.Fori(1, FCH) as c:
                    first = base + c * PER_FF + (P_LOOP - PER_FF)
                    for w, at in ((w_gate, 0), (w_up, PPG)):
                        for q in range(PPG):
                            load_pair(q % RING, first + (at + q),
                                      w[one, 2 * q * P:2 * (q + 1) * P, bass.ds(c * N, N)])
                    for q in range(DOWN):
                        n, k = q // 2, 2 * (q % 2)
                        load_pair(q % RING, first + (2 * PPG + q),
                                  w_down[one, bass.ds(c * N + (k * P - N), 2 * P), n * N:(n + 1) * N])
                for q in range(DOWN):
                    n, r = q // 2, (FCH - 1) * N + 2 * (q % 2) * P
                    load_pair(q % RING, base + (P_LAST + q), w_down[one, r:r + 2 * P, n * N:(n + 1) * N])
            for n in range(DCH):
                sp.wait_ge(dve_evac, DEPTH * EV_DVE + n + 1)
                sp.dma_start(out[0, :, n * N:(n + 1) * N].rearrange("(t p) d -> p t d", p=P),
                             xr[:, :, n * N:(n + 1) * N]).then_inc(stored, 16)
            sp.wait_ge(stored, DCH * 16)

        @block.gpsimd
        def _(pool):
            own = Steps(pool, pool_step, POOL_STEPS)

            def once(ins, n=[0]):
                n[0] += 1
                ins.then_inc(set_up, 1)
                pool.wait_ge(set_up, n[0])

            for s, credit in ((lo_split, RING), (pair_used, RING), (dve_evac, DCH)):
                pool.memset(numbers[:, 5:6], 0.0).then_inc(s, credit)
                once(pool.memset(numbers[:, 6:7], 0.0))
            once(pool.memset(ident[:, :], 0.0))
            once(pool.affine_select(out=ident[:, :], in_=ident[:, :], compare_op=ALU.not_equal, fill=1.0, base=0,
                                    pattern=[[-1, P]], channel_multiplier=1))
            pool.memset(numbers[:, 7:8], 0.0).then_inc(ident_ready, 1)
            once(pool.memset(ones[:, :], 1.0))
            once(pool.affine_select(out=tri[:, :], in_=ones[:, :], compare_op=ALU.is_ge, fill=0.0, base=0,
                                    pattern=[[1, P]], channel_multiplier=-1))
            once(pool.tensor_copy(identb[:, :], ident[:, :]))
            load_x(pool, 1)
            once(pool.memset(maskb[:, :, :], 0.0))
            once(pool.affine_select(out=maskb[:, :, :], in_=maskb[:, :, :], compare_op=ALU.is_ge, fill=NEG, base=0,
                                    pattern=[[0, HPG], [1, P]], channel_multiplier=-1))
            once(pool.iota(dist[:, 0:P], pattern=[[1, P]], base=0, channel_multiplier=-1,
                           allow_small_or_imprecise_dtypes=True))
            once(pool.iota(dist[:, P:3 * P], pattern=[[1, 2 * P]], base=-P, channel_multiplier=-1,
                           allow_small_or_imprecise_dtypes=True))
            once(pool.affine_select(out=dist[:, 0:P], in_=dist[:, 0:P], compare_op=ALU.is_ge, fill=NEG, base=0,
                                    pattern=[[-1, P]], channel_multiplier=1))
            once(pool.affine_select(out=dist[:, P:3 * P], in_=dist[:, P:3 * P], compare_op=ALU.is_ge, fill=NEG,
                                    base=P, pattern=[[-1, 2 * P]], channel_multiplier=1))
            once(pool.affine_select(out=dist[:, P:3 * P], in_=dist[:, P:3 * P], compare_op=ALU.is_gt, fill=NEG,
                                    base=0, pattern=[[1, 2 * P]], channel_multiplier=-1))
            for i, value in enumerate([1.0 / n for n in MEANS] + [EPS, -0.5]):
                once(pool.memset(numbers[:, i:i + 1], value))
            once(pool.memset(vaug[:, :, :, HEAD:HEAD + 1], 1.0))
            load_x(pool, 2)
            once(pool.memset(cpart[:, :, :, :], 0.0))
            once(pool.tensor_tensor(crest[:, 0, :], ident[:, 0:HS], ident[:, PIECE:PIECE + HS], ALU.add))
            once(pool.tensor_tensor(pick[:, :], crest[:, 0, :], ident[:, 2 * PIECE:2 * PIECE + HS], ALU.add))
            once(pool.memset(wdt_s[:, KT * 2 * HS:].bitcast(F32), 0.0))
            load_x(pool, 3)
            pool.memset(numbers[:, 7:8], 0.0).then_inc(const_ready, 1)

            with pool.Fori(0, DEPTH) as layer:
                one = bass.ds(layer, 1)
                for dst, src in ((dtb, dt_bias), (alog, a_log), (dskip, d_skip), (sink, sinks)):
                    pool.dma_start(dst[:, :], src[one, :].partition_broadcast(P)).then_inc(params_landed, 16)
                pool.dma_start(wdt[:, :, :], w_in[one, :, DT_COL:DT_COL + HS].rearrange("o (k p) n -> p (o k) n", p=P)) \
                    .then_inc(params_landed, 16)

                def power(out_, v, total, n, done):
                    def const(i):
                        c = numbers[:, i:i + 1]
                        return c.broadcast_to([P, v.shape[1]]) if len(v.shape) == 2 else \
                            c.unsqueeze(2).broadcast_to([P, v.shape[1], v.shape[2]])

                    own.done(layer, pool.tensor_tensor(v, total, const(MEANS.index(n)), ALU.mult))
                    own.done(layer, pool.tensor_tensor(v, v, const(3), ALU.add))
                    done(pool.tensor_tensor(out_, v, const(4), ALU.pow))

                pool.wait_ge(x_sums, layer * 2 + 1)
                power(rs[:, :], rsv[:, :], xsum[:, :], D, lambda i: i.then_inc(rs_ready, 1))

                def norm_qk(k):
                    st = stage[:, k % 2]
                    heads = HKV if k == 0 else 8
                    pool.wait_ge(qk_sums, layer * 3 + k + 1)
                    power(rq[:, :, 0:heads], rqv[:, :, 0:heads], ssq[:, :, 0:heads], HEAD,
                          lambda i: own.done(layer, i))
                    for t in range(T):
                        scale = rq[:, t, 0:heads].unsqueeze(2).broadcast_to([P, heads, HEAD])
                        src = st[:, t, 0:heads * HEAD].rearrange("p (h d) -> p h d", d=HEAD)
                        if k == 0:
                            for twice in range(2):
                                dst = acc[:, 2 * t:2 * t + 2, :].rearrange("p a (j w d) -> p (a j) w d", w=2, d=HEAD)
                                last = pool.tensor_tensor(dst[:, :, twice, :], src, scale, ALU.mult)
                        else:
                            last = pool.tensor_tensor(src, src, scale, ALU.mult)
                    last.then_inc(qk_scaled, 1)

                def scan_inputs(u):
                    g, c = u // 2, u % 2
                    b = u % 2
                    cols, hs = slice(g * GW, (g + 1) * GW), slice(g * HPG, (g + 1) * HPG)

                    def spread(v):
                        return v.unsqueeze(2).broadcast_to([P, HPG, HEAD])

                    def heads(v):
                        return v.rearrange("p (h d) -> p h d", d=HEAD)

                    if u == 0:
                        pool.wait_ge(tok_ready, layer * 3 + 2)
                        pool.wait_ge(dta_ready, layer * 2 + 1)
                        pool.wait_ge(ecum_ready, layer * 1 + 1)
                        own.done(layer, pool.tensor_tensor(dte[:, :], dte[:, :], dt[:, 0, :], ALU.mult))
                    if u >= 2:
                        pool.wait_ge(y_ready, layer * 8 + (u - 1))
                    x_in = heads(ys[:, c, cols])
                    pool.tensor_tensor(heads(xdt[:, b, :]), x_in, spread(dt[:, c, hs]), ALU.mult).then_inc(xdt_ready, 1)
                    if c == 0:
                        pool.tensor_tensor(heads(xde[:, :]), x_in, spread(dte[:, hs]), ALU.mult).then_inc(xdt_ready, 1)
                    pool.tensor_tensor(heads(dx[:, b, :]), x_in, spread(dskip[:, hs]), ALU.mult).then_inc(xdt_ready, 1)

                def gate(z):
                    part = slice(z * N, (z + 1) * N)
                    pool.wait_ge(act_evac, layer * EV_ACT + (8 + z))
                    pool.wait_ge(y_ready, layer * 8 + 8)
                    pool.tensor_tensor(ys[:, :, part], ys[:, :, part], stage[:, 1 - z, :, :], ALU.mult) \
                        .then_inc(gated, 1)
                    pool.wait_ge(g_squares, layer * 2 + z + 1)
                    power(rg[:, :, :], rgv[:, :, :], ssg[:, z, :, :], GW, lambda i: own.done(layer, i))
                    for t in range(T):
                        v = ys[:, t, part].rearrange("p (g d) -> p g d", d=GW)
                        last = pool.tensor_tensor(v, v, rg[:, t, :].unsqueeze(2).broadcast_to([P, 2, GW]), ALU.mult)
                        last.then_inc(g_normed, 1)

                for u in (0, 1):
                    scan_inputs(u)
                norm_qk(0)
                for u in (2, 3, 4, 5):
                    scan_inputs(u)
                norm_qk(1)
                for u in (6, 7):
                    scan_inputs(u)
                norm_qk(2)
                for z in range(2):
                    gate(z)
                pool.wait_ge(x_sums, layer * 2 + 2)
                power(rs[:, :], rsv[:, :], xsum[:, :], D, lambda i: i.then_inc(rs_ready, 1))
            own.check()

        @block.tensor
        def _(pe):
            def products(slot, pair, rows, bank, lhs_hi, lhs_lo, first, last):
                pe.wait_ge(lo_split, pair + (1 + RING))
                for k in range(2):
                    for lhs, w in ((lhs_hi, w_hi), (lhs_lo, w_hi), (lhs_hi, w_lo)):
                        for t in range(T):
                            done = nc.tensor.matmul(ps[:, bank + t, :], lhs[:, rows + k, t * P:(t + 1) * P],
                                                    w[:, slot, k, :],
                                                    start=(first and k == 0 and w is w_hi and lhs is lhs_hi),
                                                    stop=(last and k == 1 and w is w_lo))
                done.then_inc(pair_used, 1)

            def turned(bank, tiles, s, parts=1):
                for i, (at, src) in enumerate(tiles):
                    done = nc.tensor.transpose(ps[0:src.shape[1], bank + at // N, at % N:at % N + src.shape[0]],
                                               src, ident[0:src.shape[0], 0:src.shape[0]])
                    if (i + 1) % (len(tiles) // parts) == 0:
                        done.then_inc(s, 1)

            def chunk_tiles(v, n=CT):
                return [(m * TOK + t * P, v(t)[:, m * P:(m + 1) * P]) for m in range(n) for t in range(T)]

            def turn_x(layer, norm, n):
                if norm == 0:
                    pe.wait_ge(x_landed[n], 16)
                    pe.wait_ge(dve_evac, layer * EV_DVE + (n + 1))
                if n >= 2:
                    pe.wait_ge(h_lo_ready, layer * 16 + (norm * 8 + 2 * (n - 1)))
                turned(4 + 2 * (n % 2), chunk_tiles(lambda t: xr[:, t, n * N:(n + 1) * N]), xT_psum, 2)

            def conv_in(layer, j):
                pe.wait_ge(act_evac, layer * EV_ACT + (j + 1))
                if j:
                    pe.wait_ge(tok_ready, layer * 3 + j)
                else:
                    pe.wait_ge(h_lo_ready, layer * 16 + 8)
                turned(4, chunk_tiles(lambda t: stage[:, j % 2, t, :]), ch_psum)

            def conv_out(layer, j):
                pe.wait_ge(silu_ready, layer * 4 + (j + 1))
                if j == B_:
                    tiles = [(g * P, bt[:, g, 0:P]) for g in range(GROUPS)]
                else:
                    tiles = [(t * N + m * P, acc[:, m, t * P:(t + 1) * P]) for t in range(T) for m in range(CT)]
                turned(4, tiles, tok_psum)

            def dt_products(layer):
                pe.wait_ge(wdt_lo_ready, layer + 1)
                for k in range(KT):
                    for h in (h_hi, h_lo):
                        done = nc.tensor.matmul(ps[:, 6, 0:TOK], wdt_s[:, k * 2 * HS:k * 2 * HS + P], h[:, k, :],
                                                start=(k == 0 and h is h_hi), stop=(k == KT - 1 and h is h_lo))
                done.then_inc(dt_psum, 1)

            def turn_dt(layer):
                pe.wait_ge(dtT_ready, layer + 1)
                turned(7, [(t * P, dtT[:, t * P:(t + 1) * P]) for t in range(T)], dt_turned)

            def cumulate(layer):
                pe.wait_ge(const_ready, 1)
                pe.wait_ge(dta_ready, layer * 2 + 2)
                for t in range(T):
                    nc.tensor.matmul(ps[:, 6, t * HS:(t + 1) * HS], tri[:, :], dta_[:, t, :], start=True, stop=True)
                nc.tensor.matmul(ps[:, 6, 2 * HS:3 * HS], ones[:, :], dta_[:, 0, :], start=True, stop=True) \
                    .then_inc(cum_psum, 1)

            def turn_cum(layer):
                pe.wait_ge(cpart_ready, layer + 1)
                for t in range(T):
                    last = nc.tensor.matmul(ps[:, 7, t * P:(t + 1) * P],
                                            cpart[:, t, :, :].rearrange("p a h -> p (a h)"), identb[:, :],
                                            start=True, stop=True)
                last.then_inc(cumT_psum, 1)

            def scan_a(layer, u):
                g, c = u // 2, u % 2
                if u == 0:
                    pe.wait_ge(silu_ready, layer * 4 + 4)
                    pe.wait_ge(cum_ready, layer + 1)
                    pe.wait_ge(cumT_ready, layer + 1)
                else:
                    pe.wait_ge(y_ready, layer * 8 + u)
                    pe.wait_ge(state_ready, layer * 4 + (u + 1) // 2)
                nc.tensor.matmul(ps[:, 6, :], identb[:, :], maskb[:, :, :].rearrange("p h l -> p (h l)"),
                                 start=True, stop=False, skip_group_check=True)
                for k in range(HPG):
                    h = g * HPG + k
                    nc.tensor.matmul(ps[:, 6, k * P:(k + 1) * P], pick[:, h:h + 1].broadcast_to([P, P]),
                                     cumT[:, c * P:(c + 1) * P], start=False, stop=(k == HPG - 1), skip_group_check=True)
                cols = slice(c * P, (c + 1) * P)
                nc.tensor.matmul(ps[:, 7, 0:P], bt[:, g, cols], ctm[:, g, cols], start=True, stop=True) \
                    .then_inc(seg_psum, 1)

            def scan_b(layer, u):
                g, c = u // 2, u % 2
                pe.wait_ge(mt_ready, layer * 8 + (u + 1))
                pe.wait_ge(xdt_ready, layer * 20 + (5 * g + 3 + 2 * c))
                for k in range(HPG):
                    nc.tensor.matmul(ps[:, 7, 2 * P + k * HEAD:2 * P + (k + 1) * HEAD], decay[:, u % 2, k, :],
                                     xdt[:, u % 2, k * HEAD:(k + 1) * HEAD], start=True, stop=True)
                if c == 0:
                    if g == 0:
                        pe.wait_ge(tok_ready, layer * 3 + 3)
                    last = nc.tensor.matmul(ps[:, 6, 0:GW], btok[:, g, :], xde[:, :], start=True, stop=True)
                else:
                    pe.wait_ge(state_ready, layer * 4 + (g + 1))
                    last = nc.tensor.matmul(ps[:, 6, 0:GW], ctm[:, g, P:2 * P], state[:, :], start=True, stop=True)
                last.then_inc(y_psum, 1)

            def turn_qk(layer, k):
                pe.wait_ge(qk_scaled, layer * 3 + (k + 1))
                if k == 2:
                    pe.wait_ge(pT_act, layer * 8 + 1)
                    pe.wait_ge(pT_dve, layer * 8 + 1)
                elif k == 1:
                    pe.wait_ge(qkT_ready, layer * 3 + 1)
                if k == 0:
                    tiles = chunk_tiles(lambda t: acc[:, 2 * t:2 * t + 2, :].rearrange("p a c -> p (a c)"))
                else:
                    tiles = chunk_tiles(lambda t: stage[:, k % 2, t, :])
                turned(4, tiles, qkT_psum)

            def scores(layer, a):
                pe.wait_ge(qkT_ready, layer * 3 + (2 if a < 4 else 3))
                if a == 0:
                    pe.wait_ge(y_ready, layer * 8 + 8)
                if a == 1:
                    pe.wait_ge(sc_ready, layer * 8 + 1)
                if a >= 2:
                    pe.wait_ge(ao_ready, layer * 8 + (a - 1))
                if a >= 3:
                    pe.wait_ge(ma_lo, layer * 8 + (a - 2))
                for half in range(2):
                    rows, j = slice(half * HEAD, (half + 1) * HEAD), 2 * a // Q_PER_KV
                    nc.tensor.matmul(ps[:, 6 + half, 0:P], qT[rows, a, 0:P], kT[rows, j, 0:P], start=True, stop=True)
                    last = nc.tensor.matmul(ps[:, 6 + half, P:3 * P], qT[rows, a, P:2 * P], kT[rows, j, :],
                                            start=True, stop=True)
                last.then_inc(sc_psum, 1)

            def turn_p(layer, a):
                pe.wait_ge(p_ready, layer * 8 + (a + 1))
                if a == 1:
                    pe.wait_ge(qkT_ready, layer * 3 + 3)
                if a:
                    pe.wait_ge(pT_act, layer * 8 + a)
                    pe.wait_ge(pT_dve, layer * 8 + a)
                turned(4, [(half * N + i * P, sc[:, a % 2, half, i * P:(i + 1) * P])
                           for half in range(2) for i in range(3)], pT_psum)

            def weigh_v(layer, a):
                pe.wait_ge(pT_act, layer * 8 + (a + 1))
                pe.wait_ge(pT_dve, layer * 8 + (a + 1))
                if a < 7:
                    pe.wait_ge(sc_ready, layer * 8 + (a + 2))
                else:
                    pe.wait_ge(ao_ready, layer * 8 + 7)
                w = HEAD + 1
                j = 2 * a // Q_PER_KV
                for half in range(2):
                    o = [ps[:, 6, (half * T + t) * w:(half * T + t + 1) * w] for t in range(T)]
                    nc.tensor.matmul(o[0], pT[:, half, 0:P], vaug[:, 0, j, :], start=True, stop=True)
                    nc.tensor.matmul(o[1], pT[:, half, P:2 * P], vaug[:, 0, j, :], start=True, stop=False)
                    last = nc.tensor.matmul(o[1], pT[:, half, 2 * P:3 * P], vaug[:, 1, j, :], start=False, stop=True)
                last.then_inc(pv_psum, 1)

            def turn_ao(layer, a):
                pe.wait_ge(ao_ready, layer * 8 + (a + 1))
                if a >= 6:
                    pe.wait_ge(ma_lo, layer * 8 + a)
                turned(7, [(t * P, ao[:, a % 2, t, :]) for t in range(T)], aoT_psum)

            def turn_g(layer, z):
                pe.wait_ge(g_normed, layer * 4 + 2 * (z + 1))
                if z:
                    pe.wait_ge(mg_lo, layer * 4 + 2)
                turned(4, chunk_tiles(lambda t: ys[:, t, z * N:(z + 1) * N]), gT_psum, 2)

            def turn_ff(bank, layer_rounds):
                pe.wait_ge(ff_ready, layer_rounds)
                turned(bank, chunk_tiles(lambda t: stage[:, 1, t, :]), ffT_psum, 2)

            pe.wait_ge(ident_ready, 1)
            for _ in range(WARM):
                nc.tensor.matmul(ps[:, 5, 0:P], ident[:, :], ident[:, :], start=True, stop=True)
            with pe.Fori(0, DEPTH) as layer:
                base = layer * PAIRS
                pe.wait_ge(rows_landed, layer * 112 + 112)
                turned(6, [(0, vrows[:, :])], vec_psum)
                turn_x(layer, 0, 0)
                pe.wait_ge(vec_ready, layer + 1)
                turn_x(layer, 0, 1)
                for g in range(G_IN):
                    if g >= 2:
                        pe.wait_ge(act_evac, layer * EV_ACT + (g - 1))
                    if 6 <= g:
                        pe.wait_ge(qk_sums, layer * 3 + (g - 5))
                    for q in range(PPG):
                        p = g * PPG + q
                        if g == 0:
                            pe.wait_ge(h_lo_ready, layer * 16 + (q + 1))
                        products(q % RING, base + p, 2 * q, 2 * (g % 2), h_hi, h_lo, q == 0, q == PPG - 1)
                        if p in (0, 2):
                            turn_x(layer, 0, 2 + p // 2)
                        if p == 7:
                            dt_products(layer)
                        if p == 10:
                            turn_dt(layer)
                        if p == 16:
                            cumulate(layer)
                        if p == 19:
                            turn_cum(layer)
                        if 8 <= p < 40 and p % 8 == 0:
                            conv_in(layer, p // 8 - 1)
                        if 14 <= p < 38 and p % 8 == 6:
                            conv_out(layer, p // 8 - 1)
                        if p in (43, 51, 59):
                            turn_qk(layer, (p - 43) // 8)
                        if 40 <= p < 56:
                            (scan_a, scan_b)[p % 2](layer, (p - 40) // 2)
                        if 59 <= p and p % 2:
                            weigh_v(layer, (p - 59) // 2)
                        if 61 <= p and p % 2:
                            turn_ao(layer, (p - 61) // 2)
                        if 56 <= p and p % 2 == 0:
                            scores(layer, (p - 56) // 2)
                        if 58 <= p and p % 2 == 0:
                            turn_p(layer, (p - 58) // 2)
                for n in range(DCH):
                    if n < 2:
                        pe.wait_ge(act_evac, layer * EV_ACT + (G_IN - 1 + n))
                    else:
                        pe.wait_ge(dve_evac, layer * EV_DVE + (n - 1 + DCH))
                    for q, r in enumerate(OUT_ROWS):
                        p = P_OUT + n * PPG + q
                        if n == 0 and r < 8:
                            pe.wait_ge(ma_lo, layer * 8 + (r + 2))
                        if n == 0 and r >= 8:
                            pe.wait_ge(mg_lo, layer * 4 + (r // 2 - 3))
                        products(q % RING, base + p, r, 2 * ((n + 1) % 2), m_hi, m_lo, q == 0, q == PPG - 1)
                        if p == 72:
                            turn_p(layer, 7)
                        if p == 73:
                            weigh_v(layer, 7)
                            turn_ao(layer, 6)
                            turn_g(layer, 0)
                        if p == 74:
                            turn_ao(layer, 7)
                        if p == 76:
                            turn_g(layer, 1)
                        if n and q == 1:
                            pe.wait_ge(dve_evac, layer * EV_DVE + (n + DCH))
                            if n == 1:
                                pe.wait_ge(mg_lo, layer * 4 + 4)
                                pe.wait_ge(ma_lo, layer * 8 + 8)
                            turn_x(layer, 1, n - 1)
                for up in range(2):
                    pe.wait_ge(dve_evac, layer * EV_DVE + (DCH - 1 + up + DCH))
                    for q in range(PPG):
                        if up == 0:
                            pe.wait_ge(h_lo_ready, layer * 16 + (8 + q + 1))
                        products(q % RING, base + (P_FF + up * PPG + q), 2 * q, 2 - 2 * up, h_hi, h_lo,
                                 q == 0, q == PPG - 1)
                        if up == 0 and q == 1:
                            pe.wait_ge(dve_evac, layer * EV_DVE + (DCH + DCH))
                            turn_x(layer, 1, DCH - 1)
                with pe.Fori(1, FCH) as c:
                    first = base + c * PER_FF + (P_LOOP - PER_FF)
                    evac = layer * EV_DVE + c * DCH + DCH
                    pe.wait_ge(dve_evac, evac - 1)
                    pe.wait_ge(act_evac, layer * EV_ACT + c + G_IN)
                    for q in range(PPG):
                        products(q % RING, first + q, 2 * q, 2, h_hi, h_lo, q == 0, q == PPG - 1)
                        if q == 2:
                            turn_ff(4, layer * FCH + c)
                    pe.wait_ge(dve_evac, evac)
                    for q in range(PPG):
                        products(q % RING, first + (PPG + q), 2 * q, 0, h_hi, h_lo, q == 0, q == PPG - 1)
                    for q in range(DOWN):
                        n = q // 2
                        if q == 0:
                            pe.wait_ge(act_evac, layer * EV_ACT + c + (G_IN + 1))
                            pe.wait_ge(ff_lo, layer * 2 * FCH + 2 * c)
                        elif q == 2:
                            pe.wait_ge(ff_ready, layer * FCH + c + 1)
                        elif q % 2 == 0:
                            pe.wait_ge(dve_evac, evac + (n - 1))
                        products(q % RING, first + (2 * PPG + q), 2 * (q % 2), 2 * ((n + 1) % 2), m_hi, m_lo,
                                 q % 2 == 0, q % 2 == 1)
                turn_ff(4, layer * FCH + FCH)
                for q in range(DOWN):
                    n = q // 2
                    if q < 2:
                        pe.wait_ge(ff_lo, layer * 2 * FCH + (2 * FCH - 1 + q))
                    if q % 2 == 0:
                        pe.wait_ge(dve_evac, layer * EV_DVE + (EV_DVE - 1 + n))
                    products(q % RING, base + (P_LAST + q), 2 * (q % 2), 2 * ((n + 1) % 2), m_hi, m_lo,
                             q % 2 == 0, q % 2 == 1)

        @block.scalar
        def _(act):
            own = Steps(act, act_step, ACT_STEPS)

            def split_hi(layer, slot, pair, turn):
                act.wait_ge(raw_landed[slot], layer * (16 * PAIRS // RING) + turn * 16)
                act.wait_ge(pair_used, pair + 1)
                nc.scalar.copy(w_hi[:, slot, :, :], raw[:, slot, :, :]).then_inc(hi_split, 1)

            def split(layer, p):
                split_hi(layer, p % RING, layer * PAIRS + p, p // RING + 1)

            def turned_hi(dst, row, bank, vec, turned_, first, s):
                for b in range(2):
                    act.wait_ge(turned_, first + b)
                    for k in range(2):
                        m = 2 * b + k
                        last = nc.scalar.activation(dst[:, row + m, :], ps[:, bank + b, k * TOK:(k + 1) * TOK],
                                                    ACT.Copy, scale=vecs[:, vec + m:vec + m + 1])
                    last.then_inc(s, 1)

            def x_hi(layer, norm, n):
                turned_hi(h_hi, CT * n, 4 + 2 * (n % 2), (V_ATTN, V_FFN)[norm] + CT * n, xT_psum,
                          layer * 16 + (norm * 8 + 2 * n + 1), h_hi_ready)

            def squares(layer, out_, src, total, last=False):
                ins = nc.scalar.activation(out_, src, ACT.Square, accum_out=total)
                if last:
                    ins.then_inc(x_squares, 1)
                else:
                    own.done(layer, ins)

            def x_square(layer, i):
                t, half = i // 2, i % 2
                for n in (2 * half, 2 * half + 1):
                    act.wait_ge(x_landed[n], 16)
                squares(layer, stage[:, 0].rearrange("p t n -> p (t n)"), xr[:, t, half * 2 * N:(half + 1) * 2 * N],
                        ssx[:, t, half:half + 1], i == 3)

            def x_chunk_squares(layer, n):
                act.wait_ge(dve_evac, layer * EV_DVE + (n + 1 + DCH))
                for t in range(T):
                    squares(layer, stage[:, 0, t, :], xr[:, t, n * N:(n + 1) * N], ssx[:, t, n:n + 1],
                            n == DCH - 1 and t == T - 1)

            def evacuate(layer, g):
                act.wait_ge(pair_used, layer * PAIRS + ((g + 1) * PPG + RING))
                if g == 0:
                    act.wait_ge(rs_ready, layer * 2 + 1)
                if 2 <= g < 6:
                    act.wait_ge(ch_psum, layer * 4 + (g - 1))
                if g == 6:
                    act.wait_ge(qk_scaled, layer * 3 + 1)
                if g in (7, 8):
                    act.wait_ge(qkT_psum, layer * 3 + (g - 5))
                width = HKV * HEAD if g == 4 else N
                for t in range(T):
                    last = nc.scalar.activation(stage[:, g % 2, t, 0:width], ps[:, 2 * (g % 2) + t, 0:width],
                                                ACT.Silu if g >= 7 else ACT.Copy, scale=rs[:, t:t + 1])
                    if g == 4:
                        last = nc.scalar.activation(vaug[:, t, :, 0:HEAD], ps[:, t, width:N]
                                                    .rearrange("p (h d) -> p h d", d=HEAD), ACT.Copy, scale=rs[:, t:t + 1])
                last.then_inc(act_evac, 1)
                if 4 <= g < 7:
                    for t in range(T):
                        v = ps[:, 2 * (g % 2) + t, 0:width]
                        last = nc.scalar.activation(v, v, ACT.Square, scale=rs[:, t:t + 1])
                    last.then_inc(qk_squares, 1)

            def silu(layer, j):
                act.wait_ge(conv_ready, layer * 4 + (j + 1))
                dst = bt if j == B_ else ctm if j == C_ else acc
                nc.scalar.activation(dst[:, :, :], acc[:, :, :], ACT.Silu).then_inc(silu_ready, 1)

            def to_tokens(layer, j):
                act.wait_ge(tok_psum, layer * 3 + (j + 1))
                if j == B_:
                    last = nc.scalar.copy(btok[:, :, :], ps[:, 4, :].rearrange("p (g s) -> p g s", g=GROUPS))
                else:
                    for t in range(T):
                        last = nc.scalar.copy(ys[:, t, j * N:(j + 1) * N], ps[:, 4 + t, :])
                last.then_inc(tok_ready, 1)

            def scale_qk(layer, k):
                act.wait_ge(qkT_psum, layer * 3 + (k + 1))
                for b in range(2):
                    dst = kT[:, 2 * b:2 * b + 2, :] if k == 0 else qT[:, 4 * (k - 1) + 2 * b:4 * (k - 1) + 2 * b + 2, :]
                    last = nc.scalar.activation(dst, ps[:, 4 + b, :].rearrange("p (a c) -> p a c", a=2), ACT.Copy,
                                                scale=vecs[:, V_K:V_K + 1] if k == 0 else qw[:, :])
                last.then_inc(qkT_ready, 1)

            def decays(layer, u):
                g, c = u // 2, u % 2
                act.wait_ge(seg_psum, layer * 8 + (u + 1))
                for k in range(HPG):
                    h = g * HPG + k
                    last = nc.scalar.activation(decay[:, u % 2, k, :], ps[:, 6, k * P:(k + 1) * P], ACT.Exp,
                                                bias=ncum[:, c, h:h + 1])
                last.then_inc(decay_ready, 1)

            def exps(layer, a):
                act.wait_ge(sc_ready, layer * 8 + (a + 1))
                for half in range(2):
                    for t in range(T):
                        v = sc[:, a % 2, half, t * P:(2 * t + 1) * P]
                        nc.scalar.activation(v, v, ACT.Exp, bias=mx[:, 2, half, t:t + 1])
                nc.scalar.activation(es[:, a % 2, :, :], mx[:, 3, :, :], ACT.Exp).then_inc(p_ready, 1)

            def p_out(layer, a):
                act.wait_ge(pT_psum, layer * 8 + (a + 1))
                nc.scalar.copy(pT[:, 0, :], ps[:, 4, 0:3 * P]).then_inc(pT_act, 1)

            def ao_hi(layer, a):
                act.wait_ge(aoT_psum, layer * 8 + (a + 1))
                nc.scalar.copy(m_hi[:, a, :], ps[:, 7, 0:TOK]).then_inc(ma_hi, 1)

            def gate_squares(layer, z):
                act.wait_ge(gated, layer * 2 + (z + 1))
                for t in range(T):
                    for g in range(2):
                        ins = nc.scalar.activation(stage[:, 1 - z, t, g * GW:(g + 1) * GW],
                                                   ys[:, t, z * N + g * GW:z * N + (g + 1) * GW], ACT.Square,
                                                   accum_out=ssg[:, z, t, g:g + 1])
                ins.then_inc(g_squares, 1)

            def g_hi(layer, z):
                turned_hi(m_hi, 8 + CT * z, 4, V_SSM + CT * z, gT_psum, layer * 4 + (2 * z + 1), mg_hi)

            def gate_evacuate(used, ff_done=None):
                act.wait_ge(pair_used, used)
                if ff_done is not None:
                    act.wait_ge(ff_ready, ff_done)
                for t in range(T):
                    last = nc.scalar.activation(stage[:, 0, t, :], ps[:, 2 + t, :], ACT.Silu, scale=rs[:, t:t + 1])
                last.then_inc(act_evac, 1)

            def ff_high(turned_):
                for b in range(2):
                    act.wait_ge(ffT_psum, turned_ + b)
                    nc.scalar.copy(m_hi[:, 2 * b:2 * b + 2, :],
                                   ps[:, 4 + b, :].rearrange("p (a c) -> p a c", a=2)).then_inc(ff_hi, 1)

            act.wait_ge(ident_ready, 1)
            nc.scalar.activation(dtx[:, 0, :], ident[:, 0:HS], ACT.Silu)
            with act.Fori(0, DEPTH) as layer:
                base = layer * PAIRS
                split(layer, 0)
                act.wait_ge(vec_psum, layer + 1)
                own.done(layer, nc.scalar.copy(vecs[:, :], ps[:, 6, 0:VROWS]))
                nc.scalar.mul(qw[:, :], vecs[:, V_Q:V_Q + 1], HEAD ** -0.5).then_inc(vec_ready, 1)
                x_hi(layer, 0, 0)
                split(layer, 1)
                x_hi(layer, 0, 1)
                split(layer, 2)
                for p in range(P_LOOP):
                    split(layer, p + LEAD)
                    if p in (0, 2):
                        x_hi(layer, 0, 2 + p // 2)
                    if p in (1, 3, 4, 5):
                        x_square(layer, (1, 3, 4, 5).index(p))
                    if p == 6:
                        act.wait_ge(params_landed, layer * 80 + 80)
                        nc.scalar.copy(wdt_parts[:, :, 0, :], wdt[:, :, :]).then_inc(wdt_hi_ready, 1)
                    if p % 8 == 7 and p < 63:
                        evacuate(layer, p // 8)
                    if p == 12:
                        act.wait_ge(dt_abs, layer + 1)
                        nc.scalar.activation(sp[:, 1, :, :], sp[:, 0, :, :], ACT.Exp, scale=-1.0)
                        nc.scalar.activation(ea[:, :], alog[:, :], ACT.Exp).then_inc(dt_exp, 1)
                    if p == 20:
                        act.wait_ge(cumT_psum, layer + 1)
                        nc.scalar.copy(cumT[:, :], ps[:, 7, 0:TOK]).then_inc(cumT_ready, 1)
                    if p == 19:
                        act.wait_ge(cum_ready, layer + 1)
                        nc.scalar.activation(ecum[:, :], cums[:, 1, :], ACT.Exp)
                        nc.scalar.activation(dte[:, :], togo[:, :], ACT.Exp).then_inc(ecum_ready, 1)
                    if 13 <= p < 38 and p % 8 == 5:
                        silu(layer, p // 8 - 1)
                    if 14 <= p < 38 and p % 8 == 6 and p // 8 - 1 < 3:
                        to_tokens(layer, p // 8 - 1)
                    if p in (43, 51, 59):
                        scale_qk(layer, (p - 43) // 8)
                    if 40 <= p < 56:
                        u = (p - 40) // 2
                        if p % 2 == 0:
                            decays(layer, u)
                        elif u % 2 == 0:
                            act.wait_ge(y_psum, layer * 8 + (u + 1))
                            nc.scalar.copy(state[:, :], ps[:, 6, 0:GW]).then_inc(state_ready, 1)
                    if 57 <= p < 73 and p % 2:
                        exps(layer, (p - 57) // 2)
                    if 58 <= p < 74 and p % 2 == 0:
                        p_out(layer, (p - 58) // 2)
                    if 61 <= p < 75 and p % 2:
                        ao_hi(layer, (p - 61) // 2)
                    if p in (63, 71):
                        evacuate(layer, p // 8)
                    if p == 74:
                        ao_hi(layer, 7)
                    if p in (64, 72):
                        gate_squares(layer, (p - 64) // 8)
                    if p in (73, 76):
                        g_hi(layer, (p - 73) // 3)
                    if p in (81, 89, 97, 105):
                        x_hi(layer, 1, (p - 81) // 8)
                    if p in (82, 90, 98, 106):
                        x_chunk_squares(layer, (p - 82) // 8)
                    if p == P_FF + PPG - 1:
                        act.wait_ge(rs_ready, layer * 2 + 2)
                        gate_evacuate(base + (P_FF + PPG + RING))
                with act.Fori(1, FCH) as c:
                    first = base + c * PER_FF + (P_LOOP - PER_FF)
                    for q in range(PER_FF):
                        s = (q + LEAD) % RING
                        act.wait_ge(raw_landed[s], layer * (16 * PAIRS // RING) + c * (16 * PER_FF // RING)
                                    + 16 * ((P_LOOP - PER_FF + q + LEAD) // RING + 1))
                        act.wait_ge(pair_used, first + (q + LEAD + 1))
                        nc.scalar.copy(w_hi[:, s, :, :], raw[:, s, :, :]).then_inc(hi_split, 1)
                        if q == 3:
                            ff_high(layer * 2 * FCH + c * 2 - 1)
                        if q == PPG - 1:
                            gate_evacuate(first + (PPG + RING), layer * FCH + c)
                ff_high(layer * 2 * FCH + 2 * FCH - 1)
                for p in range(P_LAST + LEAD, PAIRS):
                    split(layer, p)
            own.check()

        @block.vector
        def _(dve):
            own = Steps(dve, dve_step, DVE_STEPS)
            v_ = nc.vector

            def split_lo(slot, pair):
                dve.wait_ge(hi_split, pair + 1)
                v_.tensor_tensor(w_lo[:, slot, :, :], raw[:, slot, :, :], w_hi[:, slot, :, :].bitcast(F32),
                                 ALU.subtract).then_inc(lo_split, 1)

            def turned_lo(dst, hi, row, bank, vec, hi_ready, first, s):
                for b in range(2):
                    dve.wait_ge(hi_ready, first + b)
                    for k in range(2):
                        m = 2 * b + k
                        last = v_.scalar_tensor_tensor(dst[:, row + m, :], ps[:, bank + b, k * TOK:(k + 1) * TOK],
                                                       vecs[:, vec + m:vec + m + 1], hi[:, row + m, :].bitcast(F32),
                                                       ALU.mult, ALU.subtract)
                    last.then_inc(s, 1)

            def x_lo(layer, norm, n):
                turned_lo(h_lo, h_hi, CT * n, 4 + 2 * (n % 2), (V_ATTN, V_FFN)[norm] + CT * n, h_hi_ready,
                          layer * 16 + (norm * 8 + 2 * n + 1), h_lo_ready)

            def x_sum(layer, norm, n):
                dve.wait_ge(x_squares, layer * 2 + (norm + 1))
                v_.tensor_reduce(xsum[:, :], ssx[:, :, 0:n], AX_X, ALU.add).then_inc(x_sums, 1)

            def wdt_low(layer):
                dve.wait_ge(wdt_hi_ready, layer + 1)
                v_.tensor_tensor(wdt_parts[:, :, 1, :], wdt[:, :, :], wdt_parts[:, :, 0, :].bitcast(F32), ALU.subtract) \
                    .then_inc(wdt_lo_ready, 1)

            def dt_out(layer):
                dve.wait_ge(const_ready, 1)
                dve.wait_ge(dt_psum, layer + 1)
                v_.tensor_copy(dtT[:, :], ps[:, 6, 0:TOK]).then_inc(dtT_ready, 1)

            def dt_in(layer):
                dve.wait_ge(dt_turned, layer + 1)
                dve.wait_ge(rs_ready, layer * 2 + 1)
                parts = ps[:, 7, 0:T * P].rearrange("p (t c) -> p t c", t=T)
                own.done(layer, v_.tensor_copy(dtx[:, :, :], parts[:, :, HS:2 * HS]))
                own.done(layer, v_.tensor_tensor(dtx[:, :, :], parts[:, :, 0:HS], dtx[:, :, :], ALU.add))
                for t in range(T):
                    last = v_.scalar_tensor_tensor(dtx[:, t, :], dtx[:, t, :], rs[:, t:t + 1],
                                                   dtb[:, :], ALU.mult, ALU.add)
                own.done(layer, last)
                v_.scalar_tensor_tensor(sp[:, 0, :, :], dtx[:, :, :], -1.0, dtx[:, :, :], ALU.mult, ALU.max) \
                    .then_inc(dt_abs, 1)

            def softplus(layer):
                dve.wait_ge(dt_exp, layer + 1)
                e, r, s, s2, q = sp[:, 1, :, :], sp[:, 2, :, :], sp[:, 3, :, :], sp[:, 4, :, :], sp[:, 5, :, :]
                own.done(layer, v_.tensor_scalar(r, e, 2.0, None, ALU.add))
                own.done(layer, v_.reciprocal(r, r))
                own.done(layer, v_.tensor_tensor(s, e, r, ALU.mult))
                own.done(layer, v_.tensor_tensor(s2, s, s, ALU.mult))
                own.done(layer, v_.tensor_scalar(q, s2, 1.0 / 17, None, ALU.mult))
                for odd in (15, 13, 11, 9, 7, 5, 3):
                    own.done(layer, v_.scalar_tensor_tensor(q, q, 1.0 / odd, s2, ALU.add, ALU.mult))
                own.done(layer, v_.scalar_tensor_tensor(q, q, 1.0, s, ALU.add, ALU.mult))
                own.done(layer, v_.tensor_scalar(r, dtx[:, :, :], 0.0, None, ALU.max))
                last = v_.scalar_tensor_tensor(dt[:, :, :], q, 2.0, r, ALU.mult, ALU.add)
                last.then_inc(dta_ready, 1)
                dve.wait_ge(dta_ready, layer * 2 + 1)
                for t in range(T):
                    last = v_.scalar_tensor_tensor(dta_[:, t, :], dt[:, t, :], -1.0, ea[:, :], ALU.mult, ALU.mult)
                last.then_inc(dta_ready, 1)

            def cum_out(layer):
                dve.wait_ge(cum_psum, layer + 1)
                own.done(layer, v_.tensor_copy(cums[:, :, :], ps[:, 6, 0:3 * HS].rearrange("p (a h) -> p a h", a=3)))
                v_.tensor_scalar(ncum[:, :, :], cums[:, 0:2, :], -1.0, None, ALU.mult)
                v_.tensor_tensor(togo[:, :], cums[:, 2, :], cums[:, 0, :], ALU.subtract).then_inc(cum_ready, 1)
                own.done(layer, v_.tensor_copy(cpart[:, :, 0, 0:HS], cums[:, 0:2, :]))
                own.done(layer, v_.tensor_tensor(crest[:, :, :], cums[:, 0:2, :], cpart[:, :, 0, 0:HS], ALU.subtract))
                own.done(layer, v_.tensor_copy(cpart[:, :, 1, 0:HS], crest[:, :, :]))
                v_.tensor_tensor(cpart[:, :, 2, 0:HS], crest[:, :, :], cpart[:, :, 1, 0:HS], ALU.subtract) \
                    .then_inc(cpart_ready, 1)

            def conv(layer, j, m):
                dve.wait_ge(ch_psum, layer * 4 + (j + 1))
                u = ps[:, 4 + m // 2, m % 2 * TOK:(m % 2 + 1) * TOK]
                tile_ = CT * j + m

                def tap(w):
                    at = V_CW + w * 16 + tile_
                    return vecs[:, at:at + 1]

                own.done(layer, v_.tensor_scalar(acc[:, m, :], u, tap(CONV_W - 1), vecs[:, V_CB + tile_:V_CB + tile_ + 1],
                                                 ALU.mult, ALU.add))
                for s in range(1, CONV_W):
                    ins = v_.scalar_tensor_tensor(acc[:, m, s:TOK], u[:, 0:TOK - s], tap(CONV_W - 1 - s),
                                                  acc[:, m, s:TOK], ALU.mult, ALU.add)
                    if s == CONV_W - 1 and m == CT - 1:
                        ins.then_inc(conv_ready, 1)
                    else:
                        own.done(layer, ins)

            def qk_sum(layer, k):
                dve.wait_ge(qk_squares, layer * 3 + (k + 1))
                if k:
                    dve.wait_ge(qk_scaled, layer * 3 + k)
                heads = HKV if k == 0 else 8
                for t in range(T):
                    last = v_.tensor_reduce(ssq[:, t, 0:heads], ps[:, 2 * (k % 2) + t, 0:heads * HEAD]
                                            .rearrange("p (h d) -> p h d", d=HEAD), AX_X, ALU.add)
                last.then_inc(qk_sums, 1)

            def mask_cb(layer, u):
                dve.wait_ge(decay_ready, layer * 8 + (u + 1))
                d = decay[:, u % 2, :, :]
                v_.tensor_tensor(d, d, ps[:, 7, 0:P].unsqueeze(1).broadcast_to([P, HPG, P]), ALU.mult) \
                    .then_inc(mt_ready, 1)

            def y_out(layer, u):
                g, c = u // 2, u % 2
                dve.wait_ge(y_psum, layer * 8 + (u + 1))
                y, d = ys[:, c, g * GW:(g + 1) * GW], dx[:, u % 2, :]
                within = ps[:, 7, 2 * P:2 * P + GW]
                if c == 0:
                    v_.tensor_tensor(y, within, d, ALU.add).then_inc(y_ready, 1)
                else:
                    own.done(layer, v_.tensor_tensor(d, within, d, ALU.add))
                    own.done(layer, v_.tensor_tensor(
                        y.rearrange("p (h d) -> p h d", d=HEAD), ps[:, 6, 0:GW].rearrange("p (h d) -> p h d", d=HEAD),
                        ecum[:, g * HPG:(g + 1) * HPG].unsqueeze(2).broadcast_to([P, HPG, HEAD]), ALU.mult))
                    v_.tensor_tensor(y, y, d, ALU.add).then_inc(y_ready, 1)

            def score(layer, a):
                dve.wait_ge(sc_psum, layer * 8 + (a + 1))
                if a:
                    dve.wait_ge(p_ready, layer * 8 + a)
                for half in range(2):
                    last = v_.scalar_tensor_tensor(sc[:, a % 2, half, :], dist[:, :], SLOPES[2 * a + half],
                                                   ps[:, 6 + half, 0:3 * P], ALU.mult, ALU.add)
                own.done(layer, last)
                for t in range(T):
                    last = v_.tensor_reduce(mx[:, 0, :, t], sc[:, a % 2, :, t * P:(2 * t + 1) * P], AX_X, ALU.max)
                own.done(layer, last)
                snk = sink[:, 2 * a:2 * a + 2].unsqueeze(2).broadcast_to([P, 2, T])
                own.done(layer, v_.tensor_tensor(mx[:, 1, :, :], mx[:, 0, :, :], snk, ALU.max))
                v_.tensor_scalar(mx[:, 2, :, :], mx[:, 1, :, :], -1.0, None, ALU.mult)
                v_.tensor_tensor(mx[:, 3, :, :], snk, mx[:, 1, :, :], ALU.subtract).then_inc(sc_ready, 1)

            def p_out(layer, a):
                dve.wait_ge(pT_psum, layer * 8 + (a + 1))
                v_.tensor_copy(pT[:, 1, :], ps[:, 5, 0:3 * P]).then_inc(pT_dve, 1)

            def normalise(layer, a):
                dve.wait_ge(pv_psum, layer * 8 + (a + 1))
                if a >= 2:
                    dve.wait_ge(aoT_psum, layer * 8 + (a - 1))
                pv = ps[:, 6, 0:2 * T * (HEAD + 1)].rearrange("p (h t e) -> p h t e", h=2, t=T)
                own.done(layer, v_.tensor_tensor(den[:, 0, :, :], pv[:, :, :, HEAD], es[:, a % 2, :, :], ALU.add))
                own.done(layer, v_.reciprocal(den[:, 1, :, :], den[:, 0, :, :]))
                v_.tensor_tensor(ao[:, a % 2, :, :].rearrange("p t (h d) -> p h t d", h=2), pv[:, :, :, 0:HEAD],
                                 den[:, 1, :, :].unsqueeze(3).broadcast_to([P, 2, T, HEAD]), ALU.mult) \
                    .then_inc(ao_ready, 1)

            def ao_lo(layer, a):
                dve.wait_ge(ma_hi, layer * 8 + (a + 1))
                v_.tensor_tensor(m_lo[:, a, :], ps[:, 7, 0:TOK], m_hi[:, a, :].bitcast(F32), ALU.subtract) \
                    .then_inc(ma_lo, 1)

            def g_lo(layer, z):
                turned_lo(m_lo, m_hi, 8 + CT * z, 4, V_SSM + CT * z, mg_hi, layer * 4 + (2 * z + 1), mg_lo)

            def add_x(used, n, bank):
                dve.wait_ge(pair_used, used)
                for t in range(T):
                    v = xr[:, t, n * N:(n + 1) * N]
                    last = v_.tensor_tensor(v, v, ps[:, bank + t, :], ALU.add)
                last.then_inc(dve_evac, 1)

            def up_evacuate(used, gate_done, turned_=None):
                dve.wait_ge(pair_used, used)
                dve.wait_ge(act_evac, gate_done)
                if turned_ is not None:
                    dve.wait_ge(ffT_psum, turned_)
                for t in range(T):
                    last = v_.scalar_tensor_tensor(stage[:, 1, t, :], ps[:, t, :], rs[:, t:t + 1], stage[:, 0, t, :],
                                                   ALU.mult, ALU.mult)
                last.then_inc(ff_ready, 1)

            def ff_low(hi_done):
                for b in range(2):
                    dve.wait_ge(ff_hi, hi_done + b)
                    v_.tensor_tensor(m_lo[:, 2 * b:2 * b + 2, :], ps[:, 4 + b, :].rearrange("p (a c) -> p a c", a=2),
                                     m_hi[:, 2 * b:2 * b + 2, :].bitcast(F32), ALU.subtract).then_inc(ff_lo, 1)

            with dve.Fori(0, DEPTH) as layer:
                base = layer * PAIRS
                split_lo(0, base)
                x_lo(layer, 0, 0)
                split_lo(1, base + 1)
                x_lo(layer, 0, 1)
                split_lo(2, base + 2)
                for p in range(P_LOOP):
                    if 58 <= p < 72 and p % 2 == 0:
                        score(layer, (p - 56) // 2)
                        p_out(layer, (p - 58) // 2)
                    split_lo((p + LEAD) % RING, base + (p + LEAD))
                    if p in (0, 2):
                        x_lo(layer, 0, 2 + p // 2)
                    if p == 6:
                        x_sum(layer, 0, 2)
                        wdt_low(layer)
                    if p == 9:
                        dt_out(layer)
                    if p == 11:
                        dt_in(layer)
                    if p == 13:
                        softplus(layer)
                    if 9 <= p < 37 and p % 8 in (1, 2, 3, 4):
                        conv(layer, p // 8 - 1, p % 8 - 1)
                    if p == 17:
                        cum_out(layer)
                    if p in (40, 48, 56):
                        qk_sum(layer, (p - 40) // 8)
                    if 40 <= p < 56:
                        (mask_cb, y_out)[p % 2](layer, (p - 40) // 2)
                    if p == 56:
                        score(layer, 0)
                    if p == 72:
                        p_out(layer, 7)
                    if 59 <= p < 75 and p % 2:
                        normalise(layer, (p - 59) // 2)
                    if 61 <= p < 75 and p % 2:
                        ao_lo(layer, (p - 61) // 2)
                    if p == 74:
                        ao_lo(layer, 7)
                    if p in (73, 76):
                        g_lo(layer, (p - 73) // 3)
                    if P_OUT <= p < P_FF and p % 8 == 7:
                        n = (p - P_OUT) // 8
                        add_x(base + (p + 1 + RING), n, 2 * ((n + 1) % 2))
                    if p in (81, 89, 97, 105):
                        x_lo(layer, 1, (p - 81) // 8)
                    if p == 106:
                        x_sum(layer, 1, DCH)
                    if p == P_LOOP - 1:
                        up_evacuate(base + (P_LOOP + RING), layer * EV_ACT + (G_IN + 1))
                with dve.Fori(1, FCH) as c:
                    first = base + c * PER_FF + (P_LOOP - PER_FF)
                    for q in range(PER_FF):
                        split_lo((q + LEAD) % RING, first + (q + LEAD))
                        if q == 3:
                            ff_low(layer * 2 * FCH + c * 2 - 1)
                        if q == 2 * PPG - 1:
                            up_evacuate(first + (2 * PPG + RING), layer * EV_ACT + c + (G_IN + 1), layer * 2 * FCH + 2 * c)
                        if q >= 2 * PPG and q % 2:
                            n = (q - 2 * PPG) // 2
                            add_x(first + (q + 1 + RING), n, 2 * ((n + 1) % 2))
                ff_low(layer * 2 * FCH + (2 * FCH - 1))
                for q in range(DOWN):
                    if q + LEAD < DOWN:
                        split_lo((q + LEAD) % RING, base + (P_LAST + q + LEAD))
                    if q % 2:
                        add_x(base + (P_LAST + q + 1 + RING), q // 2, 2 * ((q // 2 + 1) % 2))
            own.check()


_INS = ['x', 'attn_norm_w', 'w_in', 'q_norm_w', 'k_norm_w', 'sinks', 'conv_w', 'conv_b', 'dt_bias', 'a_log',
        'd_skip', 'ssm_norm_w', 'w_out', 'ffn_norm_w', 'w_gate', 'w_up', 'w_down']


def kernel(**inputs):
    import numpy as _np
    import concourse.bacc as _bacc
    from concourse import mybir as _mybir
    from concourse.bass_utils import run_bass_kernel_spmd as _run

    nc = _bacc.Bacc("TRN2", target_bir_lowering=False, num_devices=1)
    arrays, args = {}, []
    for name in _INS:
        a = _np.ascontiguousarray(inputs[name])
        arrays[f"in_{name}_dram"] = a
        args.append(nc.dram_tensor(f"in_{name}_dram", a.shape, _mybir.dt.from_np(a.dtype), kind="ExternalInput").ap())
    shape = inputs['x'].shape
    args.append(nc.dram_tensor("out_0_dram", shape, _mybir.dt.float32, kind="ExternalOutput").ap())
    hybrid_decoder(nc, *args)
    r = _run(nc, [arrays], core_ids=[0])
    return r.results[0]["out_0_dram"]
```
